# Optimizing a Trainium2 kernel written in Bass

```python
import jax, jax.numpy as jnp
from jax import lax
import numpy as np

D_MODEL = 2048
BATCH = 1
SEQ = 512
DEPTH = 1

SB_HEADS = 8
SB_HEAD_DIM = 128
SB_WIDTH = SB_HEADS * SB_HEAD_DIM
SB_BLOCK = 128
HG_HEADS = 8
HG_KEY_DIM = 128
HG_VAL_DIM = 128
HG_K_WIDTH = HG_HEADS * HG_KEY_DIM
HG_V_WIDTH = HG_HEADS * HG_VAL_DIM
HG_CHUNK = 64
IN_COLS = 3 * SB_WIDTH + 2 * HG_K_WIDTH + 2 * HG_V_WIDTH + 2 * D_MODEL
D_FF = 5632
CONV_WIDTH = 3
EPS = 1e-6

kernel_name = "hybrid_stickbreaking_hgrn2_convffn"

def rmsnorm(x, g):
    xf = x.astype(jnp.float32)
    y = xf * lax.rsqrt(jnp.mean(xf * xf, axis=-1, keepdims=True) + EPS)
    return (y * g.astype(jnp.float32)).astype(x.dtype)

def split_heads(a, n_heads):
    b, s, w = a.shape
    return a.reshape(b, s, n_heads, w // n_heads).transpose(0, 2, 1, 3)

def merge_heads(a):
    b, h, s, d = a.shape
    return a.transpose(0, 2, 1, 3).reshape(b, s, h * d)

def stick_breaking_attention(q, k, v):
    seq = q.shape[2]
    scale = SB_HEAD_DIM ** -0.5
    outs = []
    for blk in range(seq // SB_BLOCK):
        t0, t1 = blk * SB_BLOCK, (blk + 1) * SB_BLOCK
        qb = q[:, :, t0:t1].astype(jnp.float32)
        kb = k[:, :, :t1].astype(jnp.float32)
        z = jnp.einsum('bhtd,bhsd->bhts', qb, kb) * scale
        t_idx = t0 + jnp.arange(SB_BLOCK)[:, None]
        s_idx = jnp.arange(t1)[None, :]
        strict = s_idx < t_idx
        log_keep = jnp.where(strict, jax.nn.log_sigmoid(-z), 0.0)
        later = lax.cumsum(log_keep, axis=3, reverse=True) - log_keep
        log_w = jnp.where(strict, jax.nn.log_sigmoid(z) + later, -jnp.inf)
        w = jnp.exp(log_w)
        outs.append(jnp.einsum('bhts,bhsd->bhtd', w, v[:, :, :t1].astype(jnp.float32)))
    return jnp.concatenate(outs, axis=2).astype(v.dtype)

def hgrn2_chunkwise(q, k, v, log_f):
    b_, h_, seq, dk = q.shape
    dv = v.shape[-1]
    n_chunks = seq // HG_CHUNK

    def to_chunks(a):
        return jnp.moveaxis(a.astype(jnp.float32).reshape(b_, h_, n_chunks, HG_CHUNK, a.shape[-1]), 2, 0)

    qc, kc, vc, gc = to_chunks(q), to_chunks(k), to_chunks(v), to_chunks(log_f)
    causal = jnp.tril(jnp.ones((HG_CHUNK, HG_CHUNK), dtype=bool))[:, :, None]

    def step(state, inp):
        qi, ki, vi, gi = inp
        b = jnp.cumsum(gi, axis=2)
        o_inter = jnp.einsum('bhtd,bhde->bhte', qi * jnp.exp(b), state)
        diff = b[:, :, :, None, :] - b[:, :, None, :, :]
        decay = jnp.exp(jnp.where(causal, diff, -jnp.inf))
        scores = jnp.einsum('bhtd,bhsd,bhtsd->bhts', qi, ki, decay)
        o_intra = jnp.einsum('bhts,bhse->bhte', scores, vi)
        b_last = b[:, :, -1:, :]
        k_dec = ki * jnp.exp(b_last - b)
        new_state = jnp.exp(b_last[:, :, 0, :])[..., None] * state + jnp.einsum('bhsd,bhse->bhde', k_dec, vi)
        return new_state, o_inter + o_intra

    state0 = jnp.zeros((b_, h_, dk, dv), jnp.float32)
    _, o = lax.scan(step, state0, (qc, kc, vc, gc))
    return jnp.moveaxis(o, 0, 2).reshape(b_, h_, seq, dv)

def causal_depthwise_conv(a, w, bias):
    seq = a.shape[1]
    a_pad = jnp.pad(a, ((0, 0), (CONV_WIDTH - 1, 0), (0, 0)))
    out = bias
    for j in range(CONV_WIDTH):
        out = out + w[j] * a_pad[:, j:j + seq]
    return out

def setup_inputs(seed: int = 0) -> dict:
    key = jax.random.key(seed)
    ks = jax.random.split(key, 16)
    f32 = jnp.float32
    nrm = lambda k, shape, s: jax.random.normal(k, shape, f32) * s
    return {
        "x": nrm(ks[0], (BATCH, SEQ, D_MODEL), 1.0),
        "g_mix": 1.0 + nrm(ks[1], (DEPTH, D_MODEL), 0.02),
        "w_in": nrm(ks[2], (DEPTH, D_MODEL, IN_COLS), D_MODEL ** -0.5),
        "g_q": 1.0 + nrm(ks[3], (DEPTH, SB_HEAD_DIM), 0.02),
        "g_k": 1.0 + nrm(ks[4], (DEPTH, SB_HEAD_DIM), 0.02),
        "lb_logits": nrm(ks[5], (DEPTH + 1, HG_K_WIDTH), 0.5),
        "g_hg_out": 1.0 + nrm(ks[6], (DEPTH, HG_VAL_DIM), 0.02),
        "p_a": nrm(ks[7], (DEPTH, SB_WIDTH, D_MODEL), SB_WIDTH ** -0.5),
        "p_b": nrm(ks[8], (DEPTH, HG_V_WIDTH, D_MODEL), HG_V_WIDTH ** -0.5),
        "w_o": nrm(ks[9], (DEPTH, D_MODEL, D_MODEL), D_MODEL ** -0.5),
        "g_ffn": 1.0 + nrm(ks[10], (DEPTH, D_MODEL), 0.02),
        "w_up": nrm(ks[11], (DEPTH, D_MODEL, 2 * D_FF), D_MODEL ** -0.5),
        "conv_w": nrm(ks[12], (DEPTH, CONV_WIDTH, 2 * D_FF), CONV_WIDTH ** -0.5),
        "conv_b": nrm(ks[13], (DEPTH, 2 * D_FF), 0.02),
        "w_down": nrm(ks[14], (DEPTH, D_FF, D_MODEL), D_FF ** -0.5),
    }

def reference(x, g_mix, w_in, g_q, g_k, lb_logits, g_hg_out, p_a, p_b, w_o,
              g_ffn, w_up, conv_w, conv_b, w_down):
    splits = [SB_WIDTH, 2 * SB_WIDTH, 3 * SB_WIDTH,
              3 * SB_WIDTH + HG_K_WIDTH, 3 * SB_WIDTH + 2 * HG_K_WIDTH,
              3 * SB_WIDTH + 2 * HG_K_WIDTH + HG_V_WIDTH,
              3 * SB_WIDTH + 2 * HG_K_WIDTH + 2 * HG_V_WIDTH,
              3 * SB_WIDTH + 2 * HG_K_WIDTH + 2 * HG_V_WIDTH + D_MODEL]
    lower_bounds = jnp.cumsum(jax.nn.softmax(lb_logits.astype(jnp.float32), axis=0), axis=0)
    h = x
    for layer in range(DEPTH):
        u = rmsnorm(h, g_mix[layer])
        proj = u @ w_in[layer]
        sb_q, sb_k, sb_v, hg_q, hg_f, hg_i, hg_og, gate_a, gate_b = jnp.split(proj, splits, axis=-1)

        q = rmsnorm(split_heads(sb_q, SB_HEADS), g_q[layer])
        k = rmsnorm(split_heads(sb_k, SB_HEADS), g_k[layer])
        v = split_heads(sb_v, SB_HEADS)
        y_a = merge_heads(stick_breaking_attention(q, k, v))

        lb = lower_bounds[layer].reshape(1, HG_HEADS, 1, HG_KEY_DIM)
        f = lb + (1.0 - lb) * jax.nn.sigmoid(split_heads(hg_f, HG_HEADS).astype(jnp.float32))
        o_b = hgrn2_chunkwise(jax.nn.silu(split_heads(hg_q, HG_HEADS)), 1.0 - f,
                              split_heads(hg_i, HG_HEADS), jnp.log(f))
        o_b = rmsnorm(o_b, g_hg_out[layer])
        y_b = (merge_heads(o_b) * jax.nn.silu(hg_og.astype(jnp.float32))).astype(h.dtype)

        m = jax.nn.sigmoid(gate_a) * (y_a @ p_a[layer]) + jax.nn.sigmoid(gate_b) * (y_b @ p_b[layer])
        h = h + m @ w_o[layer]

        up = rmsnorm(h, g_ffn[layer]) @ w_up[layer]
        up = causal_depthwise_conv(up, conv_w[layer], conv_b[layer])
        gate, val = jnp.split(up, 2, axis=-1)
        h = h + (jax.nn.silu(gate) * val) @ w_down[layer]
    return h


_drawn_inputs = setup_inputs


def setup_inputs(seed=0):
    import zlib

    import numpy as np

    out = dict(_drawn_inputs(seed))
    spreads = {}
    factors = {'g_mix': 4.102,
     'g_q': 28.393,
     'g_k': 26.674,
     'lb_logits': 2.908,
     'g_hg_out': 8.0,
     'g_ffn': 13.263,
     'conv_b': 13.085}
    for name, (base, spread) in spreads.items():
        noise = np.random.default_rng([zlib.crc32(name.encode()), seed]).standard_normal(out[name].shape)
        drawn = base * np.exp(spread * noise) if base else spread * noise
        out[name] = __import__('jax').numpy.asarray(drawn.astype(out[name].dtype))
    for name, factor in factors.items():
        out[name] = (out[name] * factor).astype(out[name].dtype)
    return out
```

```python
import numpy as np
import concourse.bass as bass
from concourse import mybir

F32 = mybir.dt.float32
F32R = mybir.dt.float32r
I32 = mybir.dt.int32
ALU = mybir.AluOpType
ACT = mybir.ActivationFunctionType

P = 128
SEQ = 512
DM = 2048
KT = DM // P
HEADS = 8
FF = 5632
FT = FF // P
EPS = 1e-6
SCALE = float(P) ** -0.5
MASKED = -(2.0 ** 100)

UK = 8
UC = UK * P
WSLOTS = 4
LEAD = 3
NB = SEQ // P
LEVELS = 7

HEAD_UNITS = 22
HEAD_TILES = 11
HEADS_PER_BODY = 2
BODY1 = HEADS_PER_BODY * HEAD_UNITS
UNITS1 = HEADS * HEAD_UNITS
UNITS2 = 2 * KT
UNITS3 = 2 * KT
GROUP = 4
GROUPS = FT // GROUP
UP_UNITS = 4 * GROUP
DOWN_UNITS = KT // 2
START2 = UNITS1
START3 = START2 + UNITS2
START4 = START3 + UNITS3
BODY4 = START4 + UP_UNITS
GROUP_UNITS = UP_UNITS + DOWN_UNITS
UNITS = START4 + GROUPS * GROUP_UNITS
LAST_DOWN = UNITS - DOWN_UNITS
TILES2 = HEADS * HEAD_TILES
TILES3 = TILES2 + 2 * KT
TILES4 = TILES3 + KT
TILES_BODY4 = TILES4 + 2 * GROUP
GROUP_TILES = 2 * GROUP + KT
TILES_LAST = TILES_BODY4 + (GROUPS - 1) * GROUP_TILES

ROW = [0, 512, 896, 1152, 1280]
P_MIX, P_FFN, P_CONV = 0, KT, 2 * KT
P_LB0 = P_CONV + 2 * FT * 4
P_LB1 = P_LB0 + HEADS
P_GQ = P_LB1 + HEADS
P_GK, P_GH = P_GQ + 1, P_GQ + 2
NPAR = P_GQ + 3
DVE_STEPS1, ACT_STEPS1 = 110, 12


class Steps:

    def __init__(self, eng, sem):
        self.eng, self.sem, self.base, self.n = eng, sem, 0, 0

    def did(self, ins):
        ins.then_inc(self.sem, 1)
        self.n += 1

    def wait(self, back=0):
        self.eng.wait_ge(self.sem, self.base + (self.n - back))


def build_program(nc, x_t, wstream, params, out_t):
    gates_dram = nc.dram_tensor("gates_scratch", (KT, 2, P, SEQ), F32, kind="Internal").ap()
    h_dram = nc.dram_tensor("h_scratch", (P, KT * SEQ), F32, kind="Internal").ap()

    base = (nc.sbuf_base + 63) // 64 * 64
    T = SEQ * 4

    def sb(name, cols, at, dt=F32):
        return nc.alloc_sbuf_tensor_at(name, [P, cols], dt, offset=base + at)

    w_raw = sb("w_raw", WSLOTS * UC, 0)
    w_hi = sb("w_hi", WSLOTS * UC, 4 * WSLOTS * UC, F32R)
    w_lo = sb("w_lo", WSLOTS * UC, 8 * WSLOTS * UC, F32R)
    R1 = 12 * WSLOTS * UC
    R2 = R1 + 2 * KT * T
    R3 = R2 + KT * T
    R4 = R3 + KT * T
    u_hi = sb("u_hi", KT * SEQ, R1, F32R)
    u_lo = sb("u_lo", KT * SEQ, R1 + KT * T, F32R)
    m_hi = sb("m_hi", KT * SEQ, R1, F32R)
    m_raw = sb("m_raw", KT * SEQ, R1 + KT * T)
    m_lo = sb("m_lo", KT * SEQ, R1 + KT * T, F32R)
    h_acc = sb("h_acc", KT * SEQ, R1)
    s_hi = sb("s_hi", 2 * GROUP * SEQ, R1 + KT * T, F32R)
    s_raw = sb("s_raw", 2 * GROUP * SEQ, R1 + KT * T + 2 * GROUP * T)
    s_lo = sb("s_lo", 2 * GROUP * SEQ, R1 + KT * T + 2 * GROUP * T, F32R)
    x_in = sb("x_in", KT * SEQ, R2)
    y_raw = sb("y_raw", KT * SEQ, R2)
    y_lo = sb("y_lo", KT * SEQ, R2, F32R)
    v_lo = sb("v_lo", KT * SEQ, R2, F32R)
    x_sq = sb("x_sq", KT * SEQ, R3)
    y_hi = sb("y_hi", KT * SEQ, R3, F32R)
    v_hi = sb("v_hi", KT * SEQ, R3, F32R)
    NZ = ROW[4]
    za = sb("za", NZ, R3)
    sp = sb("sp", NZ, R3 + 4 * NZ)
    sp_lo = sb("sp_lo", NZ, R3 + 4 * NZ, F32R)
    sp_hi = sb("sp_hi", NZ, R3 + 8 * NZ, F32R)
    xl = sb("xl", LEVELS * SEQ, R3)
    at = R3 + 12 * NZ
    S = sb("S", NB * SEQ, at)
    cq = sb("cq", 6 * P, at + NB * T)
    kc = sb("kc", SEQ, at + NB * T + 4 * 6 * P)
    pre = sb("pre", SEQ, at + NB * T + 4 * 6 * P + T)
    suf = sb("suf", SEQ, at + NB * T + 4 * 6 * P + 2 * T)
    assert at + NB * T + 4 * 6 * P + 3 * T <= R4

    tile = [R4 + j * T for j in range(12)]
    qn, kn, v_in, v_tok = (sb(n, SEQ, tile[j]) for j, n in enumerate(("qn", "kn", "v_in", "v_tok")))
    sq, ms, rs, tmp, r_tok, og = (sb(n, SEQ, tile[4 + j]) for j, n in
                                  enumerate(("sq", "ms", "rs", "tmp", "r_tok", "og")))
    g_out = [sb(f"g_out{j}", SEQ, tile[10 + j]) for j in range(2)]
    g_in = [sb(f"g_in{j}", 2 * SEQ, tile[2 * j]) for j in range(2)]
    xr = [sb(f"xr{j}", SEQ, tile[j]) for j in range(2)]
    hb = [sb(f"hb{j}", SEQ, tile[10 + j]) for j in range(2)]
    PAD = 2
    a_pad = [sb("a_gate", SEQ + PAD, tile[0]), sb("a_val", SEQ + PAD, tile[0] + T + 32)]
    y_gate, y_val = sb("y_gate", SEQ, tile[3]), sb("y_val", SEQ, tile[4])
    c0 = R4 + 12 * T
    par = sb("par", NPAR, c0)
    c0 = (c0 + 4 * NPAR + 31) // 32 * 32
    lb = sb("lb", 4 * HEADS, c0)
    c0 += 16 * HEADS
    gq_s = sb("gq_s", 1, c0)
    wait_cell = sb("wait_cell", 1, c0 + 32)
    c0 += 64
    ident = sb("ident", P, c0)
    ones = sb("ones", P, c0 + 4 * P)
    ntri_r = sb("ntri_r", P, c0 + 8 * P, F32R)
    nones_r = sb("nones_r", P, c0 + 12 * P, F32R)
    ident_r = sb("ident_r", P, c0 + 16 * P, F32R)
    nmask_r = sb("nmask_r", P, c0 + 20 * P, F32R)
    lmask = sb("lmask", LEVELS * 64, c0 + 24 * P)
    assert base + c0 + 24 * P + 4 * LEVELS * 64 <= nc.sbuf_usable_end
    ntri, nones, nmask = (sb(n, P, tile[j]) for j, n in enumerate(("ntri", "nones", "nmask")))

    bank = [nc.alloc_psum_tensor(f"bank{j}", [P, SEQ], F32) for j in range(8)]
    Z = bank[2:6]
    misc_a, misc_b = bank[6], bank[7]
    BANKS2, BANKS3 = [2, 3, 4, 5], [6, 7, 0, 1]
    BANKS4 = [2, 3, 4, 5, 6, 7, 0, 1]

    sem = nc.alloc_semaphore
    w_in_slot = [sem(f"w_in_slot{j}") for j in range(WSLOTS)]
    w_hi_ready, w_ready = sem("w_hi_ready"), sem("w_ready")
    unit_done = sem("unit_done")
    tile_out = sem("tile_out")
    par_in = sem("par_in")
    x_arrived = [sem(f"x_arrived{j}") for j in range(8)]
    const_step, const_ready = sem("const_step"), sem("const_ready")
    u_hi_ready, u_ready, x_sq_ready = sem("u_hi_ready"), sem("u_ready"), sem("x_sq_ready")
    sumsq_ready, rms_sum, rms_ms, rms_rs, rms_step = (
        sem(n) for n in ("sumsq_ready", "rms_sum", "rms_ms", "rms_rs", "rms_step"))
    lb_exp, lb_max = sem("lb_exp"), sem("lb_max")
    sq_ready, ssq_done, ms_ready, rs_ready = sem("sq_ready"), sem("ssq_done"), sem("ms_ready"), sem("rs_ready")
    qk_ready, vt_done, vt_ready = sem("qk_ready"), sem("vt_done"), sem("vt_ready")
    z_done, log1p_ready, sp_ready = sem("z_done"), sem("log1p_ready"), sem("sp_ready")
    sp_hi_ready, sp_lo_ready, c_done, prob_ready = (
        sem("sp_hi_ready"), sem("sp_lo_ready"), sem("c_done"), sem("prob_ready"))
    mix_done, sig_ready, silu_done = sem("mix_done"), sem("sig_ready"), sem("silu_done")
    xl_ready, lev_done, sel_ready, cross_ready = (
        sem("xl_ready"), sem("lev_done"), sem("sel_ready"), sem("cross_ready"))
    yb_ready = sem("yb_ready")
    gate_stored = [sem(f"gate_stored{j}") for j in range(2)]
    y_hi_ready, y_ready = sem("y_hi_ready"), sem("y_ready")
    gate_in = [sem(f"gate_in{j}") for j in range(2)]
    gate_sig, m_raw_ready, m_hi_ready, m_ready = (
        sem("gate_sig"), sem("m_raw_ready"), sem("m_hi_ready"), sem("m_ready"))
    xr_in = [sem(f"xr_in{j}") for j in range(2)]
    h_stored = [sem(f"h_stored{j}") for j in range(2)]
    v_hi_ready, v_ready, h_sq_ready = sem("v_hi_ready"), sem("v_ready"), sem("h_sq_ready")
    h_back = sem("h_back")
    pad_ready, conv_start, conv_ready, silu_ready = (
        sem("pad_ready"), sem("conv_start"), sem("conv_ready"), sem("silu_ready"))
    s_raw_ready, s_hi_ready, s_ready = sem("s_raw_ready"), sem("s_hi_ready"), sem("s_ready")
    out_stored = sem("out_stored")
    act_step, dve_step = sem("act_step"), sem("dve_step")

    def cols(t, j, n=SEQ):
        return t[:, bass.ds(j * n, n)] if not isinstance(j, int) else t[:, j * n:(j + 1) * n]

    def col(t, j):
        return t[:, bass.ds(j, 1)] if not isinstance(j, int) else t[:, j:j + 1]

    def diagonal(m):
        a = S[:, 0:1]
        if m == 0:
            return bass.AP(tensor=a.tensor, offset=a.offset, ap=[list(a.ap[0]), [SEQ + P, NB], [1, P]])
        return bass.AP(tensor=a.tensor, offset=a.offset + m,
                       ap=[list(a.ap[0]), [SEQ + P, NB], [2 * m, 64 // m], [1, m]])

    def halves(t, m, c=SEQ):
        return t[:, 0:c].rearrange("p (g two r) -> p g two r", two=2, r=m)

    LEVEL_AT = {0: (0, 0), 1: (0, 256), 2: (1, 0), 3: (1, 256), 4: (0, 0), 5: (0, 256), 6: (1, 0)}
    ROUND = [(0, 1, 2, 3), (4, 5, 6)]

    with nc.Block() as block:

        @block.sync
        def _(sp_):
            def load_unit(n, slot):
                sp_.dma_start(w_raw[:, slot * UC:(slot + 1) * UC], wstream[n, :, :]
                              if isinstance(n, int) else wstream[bass.ds(n, 1), :, :]
                              .rearrange("o p c -> (o p) c")).then_inc(w_in_slot[slot], 16)

            XC = KT * SEQ // 8
            for c in range(4):
                load_unit(c, c)
                for e in (2 * c, 2 * c + 1):
                    sp_.dma_start(x_in[:, e * XC:(e + 1) * XC], x_t[:, e * XC:(e + 1) * XC]).then_inc(x_arrived[e], 16)
            with sp_.Fori(1, UNITS // WSLOTS) as r:
                for slot in range(WSLOTS):
                    sp_.wait_ge(w_ready, r * WSLOTS + (slot + 1 - WSLOTS))
                    load_unit(r * WSLOTS + slot, slot)
            for d in range(DOWN_UNITS):
                sp_.wait_ge(tile_out, 2 + TILES_LAST + 2 * d + 2)
                sp_.dma_start(out_t[:, 2 * d * SEQ:(2 * d + 2) * SEQ],
                              h_acc[:, 2 * d * SEQ:(2 * d + 2) * SEQ]).then_inc(out_stored, 16)
            sp_.wait_ge(out_stored, 16 * DOWN_UNITS)

        @block.gpsimd
        def _(pool):
            pool.dma_start(par[:, :], params).then_inc(par_in, 16)
            n = 0

            def step(ins):
                nonlocal n
                ins.then_inc(const_step, 1)
                n += 1
                pool.wait_ge(const_step, n)

            step(pool.memset(ones[:, :], 1.0))
            step(pool.memset(nones[:, :], -1.0))
            step(pool.memset(nmask[:, :], MASKED))
            step(pool.affine_select(out=ident[:, :], in_=ones[:, :], compare_op=ALU.is_equal, fill=0.0,
                                    base=0, pattern=[[-1, P]], channel_multiplier=1))
            step(pool.affine_select(out=ntri[:, :], in_=nones[:, :], compare_op=ALU.is_ge, fill=0.0,
                                    base=0, pattern=[[-1, P]], channel_multiplier=1))
            step(pool.affine_select(out=nmask[:, :], in_=nmask[:, :], compare_op=ALU.is_ge, fill=0.0,
                                    base=0, pattern=[[-1, P]], channel_multiplier=1))
            for L in range(LEVELS):
                m, g = 1 << L, 64 >> L
                mv = lmask[:, L * 64:(L + 1) * 64].rearrange("p (j r) -> p j r", j=g)
                ov = ones[:, 0:64].rearrange("p (j r) -> p j r", j=g)
                step(pool.affine_select(out=mv, in_=ov, compare_op=ALU.is_ge, fill=0.0,
                                        base=0, pattern=[[-2 * m, g], [0, m]], channel_multiplier=1))
                step(pool.affine_select(out=mv, in_=mv, compare_op=ALU.is_ge, fill=0.0,
                                        base=m - 1, pattern=[[2 * m, g], [0, m]], channel_multiplier=-1))
            pool.sem_inc(const_ready, 1)

            with pool.Fori(0, HEADS) as h:
                for k in range(4):
                    j, which = k % 2, k // 2
                    pool.wait_ge(tile_out, h * HEAD_TILES + (2 + 7 + k + 1))
                    pool.dma_start(gates_dram[bass.ds(h * 2 + j, 1), which, :, :].rearrange("o p c -> (o p) c"),
                                   g_out[j][:, :]).then_inc(gate_stored[j], 16)
            for j in range(2):
                pool.wait_ge(gate_stored[j], 16 * 2 * HEADS)

            def load_gates(c, j):
                src = gates_dram[c, :, :, :] if isinstance(c, int) else \
                    gates_dram[bass.ds(c, 1), :, :, :].rearrange("o a p c -> (o a) p c")
                pool.dma_start(g_in[j][:, :].rearrange("p (a c) -> p a c", a=2),
                               src.rearrange("a p c -> p a c")).then_inc(gate_in[j], 16)
            for j in range(2):
                load_gates(j, j)
            with pool.Fori(1, KT // 2) as r:
                for j in range(2):
                    pool.wait_ge(m_raw_ready, r * 2 + (j - 1))
                    load_gates(r * 2 + j, j)

            for j in range(2):
                pool.wait_ge(m_raw_ready, KT)
                pool.dma_start(xr[j][:, :], x_t[:, j * SEQ:(j + 1) * SEQ]).then_inc(xr_in[j], 16)
            with pool.Fori(0, KT // 2 - 1) as r:
                for j in range(2):
                    pool.wait_ge(tile_out, r * 2 + (2 + TILES3 + j + 1))
                    pool.dma_start(cols(h_dram, r * 2 + j), hb[j][:, :]).then_inc(h_stored[j], 16)
                    pool.dma_start(xr[j][:, :], cols(x_t, r * 2 + (j + 2))).then_inc(xr_in[j], 16)
            for j in range(2):
                c = KT - 2 + j
                pool.wait_ge(tile_out, 2 + TILES3 + c + 1)
                pool.dma_start(cols(h_dram, c), hb[j][:, :]).then_inc(h_stored[j], 16)
            for j in range(2):
                pool.wait_ge(h_stored[j], 16 * KT // 2)
            pool.wait_ge(unit_done, WSLOTS + START4)
            pool.dma_start(h_acc[:, :], h_dram).then_inc(h_back, 16)

        @block.scalar
        def _(act):
            steps = Steps(act, act_step)

            def split_hi(n, slot, arrived):
                act.wait_ge(w_in_slot[slot], arrived)
                act.wait_ge(unit_done, n + 1)
                act.activation(w_hi[:, slot * UC:(slot + 1) * UC], w_raw[:, slot * UC:(slot + 1) * UC],
                               ACT.Copy).then_inc(w_hi_ready, 1)

            def split_ahead(start, i, body, p):
                q = p + LEAD
                if isinstance(i, int):
                    n = start + i * body + q
                    if n < UNITS:
                        split_hi(n, n % WSLOTS, 16 * (n // WSLOTS + 1))
                else:
                    assert start % WSLOTS == 0 and body % WSLOTS == 0
                    split_hi(i * body + (start + q), q % WSLOTS,
                             i * (16 * body // WSLOTS) + 16 * ((start + q) // WSLOTS + 1))

            act.wait_ge(par_in, 16)
            XC = KT * SEQ // 4

            def squares(c):
                act.activation(x_sq[:, c * XC:(c + 1) * XC], x_in[:, c * XC:(c + 1) * XC],
                               ACT.Square).then_inc(x_sq_ready, 1)

            split_hi(0, 0, 16)
            for c in range(4):
                for k in range(4 * c, 4 * c + 4):
                    if k % 2 == 0:
                        act.wait_ge(x_arrived[k // 2], 16)
                    act.activation(cols(u_hi, k), cols(x_in, k), ACT.Copy,
                                   scale=col(par, P_MIX + k)).then_inc(u_hi_ready, 1)
                if c < LEAD - 1:
                    split_hi(c + 1, c + 1, 16)
                if c > 0:
                    squares(c - 1)
            squares(3)
            act.wait_ge(lb_max, 2)
            act.activation(lb[:, 0:2 * HEADS], lb[:, 2 * HEADS:4 * HEADS], ACT.Exp).then_inc(lb_exp, 1)

            def inv_sqrt_start(ready, value, done):
                act.wait_ge(ready, value)
                steps.did(act.activation(rs[:, :], ms[:, :], ACT.Ln))
                steps.wait()
                act.activation(rs[:, :], rs[:, :], ACT.Exp, scale=-0.5).then_inc(done, 1)

            def phase1_body(i):
                for hh in range(HEADS_PER_BODY):
                    def per(a, b):
                        return i * (HEADS_PER_BODY * a) + (hh * a + b)

                    def tile_ready(t):
                        act.wait_ge(tile_out, per(HEAD_TILES, 2 + t + 1))

                    late = int(isinstance(i, int) and hh == 0)
                    for p in range(HEAD_UNITS):
                        split_ahead(0, i, BODY1, hh * HEAD_UNITS + p)
                        if p == 1 + late:
                            if late:
                                inv_sqrt_start(rms_ms, 1, rms_rs)
                            tile_ready(0)
                            act.activation(sq[:, :], qn[:, :], ACT.Square).then_inc(sq_ready, 1)
                        if p == 2 + late:
                            inv_sqrt_start(ms_ready, per(3, 1), rs_ready)
                        if p == 3:
                            tile_ready(1)
                            act.activation(sq[:, :], kn[:, :], ACT.Square).then_inc(sq_ready, 1)
                        if p == 4:
                            inv_sqrt_start(ms_ready, per(3, 2), rs_ready)
                        if p == 6:
                            act.wait_ge(vt_done, per(2, 1))
                            act.activation(v_tok[:, :], misc_b[:, :], ACT.Copy).then_inc(vt_ready, 1)
                            act.wait_ge(z_done, per(1, 1))
                            for b in range(NB):
                                ins = act.activation(za[:, ROW[b]:ROW[b + 1]], Z[b][:, b * P:SEQ], ACT.Abs)
                            steps.did(ins)
                            steps.wait()
                            steps.did(act.activation(za[:, :], za[:, :], ACT.Exp, scale=-1.0))
                            steps.wait()
                            act.activation(za[:, :], za[:, :], ACT.Ln, bias=1.0).then_inc(log1p_ready, 1)
                        if p == 7:
                            act.wait_ge(sp_ready, per(1, 1))
                            act.activation(sp_hi[:, :], sp[:, :], ACT.Copy).then_inc(sp_hi_ready, 1)
                        if p == 9:
                            act.wait_ge(c_done, per(1, 1))
                            for b in range(NB):
                                ins = act.activation(S[:, b * SEQ + b * P:(b + 1) * SEQ], Z[b][:, b * P:SEQ], ACT.Exp)
                            ins.then_inc(prob_ready, 1)
                            tile_ready(3)
                            act.activation(pre[:, :], pre[:, :], ACT.Sigmoid).then_inc(sig_ready, 1)
                            tile_ready(4)
                            act.activation(rs[:, :], qn[:, :], ACT.Sigmoid).then_inc(sig_ready, 1)
                        if p == 10:
                            act.wait_ge(mix_done, per(2, 1))
                            act.activation(cols(y_raw, per(1, 0)), misc_a[:, :], ACT.Copy).then_inc(act_step, 1)
                            steps.n += 1
                        if p == 12:
                            act.wait_ge(vt_done, per(2, 2))
                            act.activation(v_tok[:, :], misc_b[:, :], ACT.Copy).then_inc(vt_ready, 1)
                        if p == 13:
                            tile_ready(6)
                            act.wait_ge(silu_done, per(2, 1))
                            act.activation(rs[:, :], og[:, :], ACT.Sigmoid).then_inc(sig_ready, 1)
                        if p == 15:
                            act.wait_ge(lev_done, per(2, 2))
                            act.activation(S[:, P:SEQ], Z[2][:, 0:3 * P], ACT.Copy)
                            act.activation(S[:, SEQ + 2 * P:2 * SEQ], Z[3][:, 0:2 * P], ACT.Copy)
                            act.activation(S[:, 2 * SEQ + 3 * P:3 * SEQ], Z[3][:, 2 * P:3 * P],
                                           ACT.Copy).then_inc(cross_ready, 1)
                        if p == 17:
                            act.wait_ge(mix_done, per(2, 2))
                            act.activation(cols(y_raw, per(1, HEADS)), misc_b[:, :], ACT.Copy)
                            act.activation(sq[:, :], misc_b[:, :], ACT.Square).then_inc(sq_ready, 1)
                        if p == 18:
                            inv_sqrt_start(ms_ready, per(3, 3), rs_ready)

            phase1_body(0)
            assert steps.n - 1 == ACT_STEPS1, steps.n
            with act.Fori(1, HEADS // HEADS_PER_BODY) as i:
                steps.base, steps.n = i * ACT_STEPS1, 1
                phase1_body(i)
                assert steps.n == ACT_STEPS1 + 1
            steps.base, steps.n = ACT_STEPS1 * (HEADS // HEADS_PER_BODY), 1

            YC = GROUP * SEQ
            for c in range(4):
                if c == 2:
                    act.wait_ge(yb_ready, HEADS)
                if c == 0:
                    steps.wait()
                act.activation(y_hi[:, c * YC:(c + 1) * YC], y_raw[:, c * YC:(c + 1) * YC],
                               ACT.Copy).then_inc(y_hi_ready, 1)
            with act.Fori(0, KT // 2) as i:
                for c in range(2):
                    for p in range(2):
                        split_ahead(START2, i, 2 * 2, 2 * c + p)
                        if p == 0:
                            act.wait_ge(gate_in[c], i * 16 + 16)
                            act.activation(g_in[c][:, :], g_in[c][:, :], ACT.Sigmoid).then_inc(gate_sig, 1)
                        if p == 1:
                            act.wait_ge(m_raw_ready, i * 2 + (c + 1))
                            act.activation(cols(m_hi, i * 2 + c), cols(m_raw, i * 2 + c),
                                           ACT.Copy).then_inc(m_hi_ready, 1)

            with act.Fori(0, KT // 2) as i:
                for c in range(2):
                    for p in range(2):
                        split_ahead(START3, i, 2 * 2, 2 * c + p)
                        if p == 1:
                            act.wait_ge(tile_out, i * 2 + (2 + TILES3 + c + 1))
                            act.activation(cols(v_hi, i * 2 + c), hb[c][:, :], ACT.Copy,
                                           scale=col(par, i * 2 + (P_FFN + c))).then_inc(v_hi_ready, 1)
                            act.wait_ge(v_ready, i * 2 + (c + 1))
                            act.activation(sq[:, :], hb[c][:, :], ACT.Square).then_inc(h_sq_ready, 1)

            def conv_term(q, t_out, which, conv_col):
                act.wait_ge(tile_out, t_out)
                y = (y_gate, y_val)[which]
                act.activation(y[:, :], a_pad[which][:, PAD:PAD + SEQ], ACT.Identity,
                               scale=col(par, conv_col + 2), bias=col(par, conv_col + 3)).then_inc(conv_start, 1)

            def up_slot(p, par_g, q0, t0):
                f, r = divmod(p, 4)
                if r == 1 and f < GROUP:
                    conv_term(q0 + f, t0 + (2 + 2 * f + 1), 0, (q0 + f) * 4 + P_CONV)
                if r == 2 and f < GROUP:
                    act.wait_ge(conv_ready, q0 + (f + 1))
                    act.activation(y_gate[:, :], y_gate[:, :], ACT.Silu).then_inc(silu_ready, 1)
                if r == 3 and f < GROUP:
                    conv_term(q0 + f, t0 + (2 + 2 * f + 2), 1, (q0 + f) * 4 + (P_CONV + 4 * FT))
                if r == 0 and f > 0:
                    k = par_g * GROUP + f - 1
                    act.wait_ge(s_raw_ready, q0 + f)
                    act.activation(cols(s_hi, k), cols(s_raw, k), ACT.Copy).then_inc(s_hi_ready, 1)

            for p in range(UP_UNITS):
                split_ahead(START4, 0, UP_UNITS, p)
                if p == 1:
                    inv_sqrt_start(rms_ms, 2, rms_rs)
                up_slot(p, 0, 0, TILES4)
            up_slot(UP_UNITS, 0, 0, TILES4)
            with act.Fori(0, (GROUPS - 1) // 2) as i:
                for gg in range(2):
                    for p in range(GROUP_UNITS):
                        split_ahead(BODY4, i, 2 * GROUP_UNITS, gg * GROUP_UNITS + p)
                        if p <= UP_UNITS:
                            up_slot(p, (1 + gg) % 2, i * (2 * GROUP) + GROUP * (1 + gg),
                                    i * (2 * GROUP_TILES) + (TILES_BODY4 + gg * GROUP_TILES))
            for p in range(DOWN_UNITS):
                split_ahead(LAST_DOWN, 0, DOWN_UNITS, p)

        @block.vector
        def _(dve):
            steps = Steps(dve, dve_step)

            def split_lo(n, slot):
                dve.wait_ge(w_hi_ready, n + 1)
                dve.tensor_tensor(w_lo[:, slot * UC:(slot + 1) * UC], w_raw[:, slot * UC:(slot + 1) * UC],
                                  w_hi[:, slot * UC:(slot + 1) * UC].bitcast(F32), ALU.subtract).then_inc(w_ready, 1)

            def split_ahead(start, i, body, p):
                q = p + LEAD
                if isinstance(i, int):
                    n = start + i * body + q
                    if n < UNITS:
                        split_lo(n, n % WSLOTS)
                else:
                    split_lo(i * body + (start + q), q % WSLOTS)

            dve.sem_inc(tile_out, 2)
            dve.wait_ge(par_in, 16)
            steps.did(dve.tensor_scalar(gq_s[:, :], col(par, P_GQ), SCALE, None, ALU.mult))
            steps.did(dve.tensor_tensor(lb[:, 0:HEADS], par[:, P_LB0:P_LB0 + HEADS],
                                        par[:, P_LB1:P_LB1 + HEADS], ALU.max))
            steps.wait()
            for j, at_ in enumerate((P_LB0, P_LB1)):
                dve.tensor_tensor(lb[:, (2 + j) * HEADS:(3 + j) * HEADS], par[:, at_:at_ + HEADS],
                                  lb[:, 0:HEADS], ALU.subtract).then_inc(lb_max, 1)
            XC = KT * SEQ // 4
            split_lo(0, 0)
            for c in range(4):
                if c == 3:
                    dve.wait_ge(x_sq_ready, 2)
                    steps.did(dve.tensor_tensor(x_sq[:, 0:XC], x_sq[:, 0:XC], x_sq[:, XC:2 * XC], ALU.add))
                for k in range(4 * c, 4 * c + 4):
                    dve.wait_ge(u_hi_ready, k + 1)
                    dve.scalar_tensor_tensor(out=cols(u_lo, k), in0=cols(x_in, k), scalar=col(par, P_MIX + k),
                                             in1=cols(u_hi, k).bitcast(F32), op0=ALU.mult,
                                             op1=ALU.subtract).then_inc(u_ready, 1)
                if c < LEAD - 1:
                    split_lo(c + 1, c + 1)
            steps.wait()
            dve.wait_ge(x_sq_ready, 4)
            steps.did(dve.tensor_tensor(x_sq[:, 0:XC], x_sq[:, 0:XC], x_sq[:, 2 * XC:3 * XC], ALU.add))
            steps.wait()
            steps.did(dve.tensor_tensor(x_sq[:, 0:XC], x_sq[:, 0:XC], x_sq[:, 3 * XC:4 * XC], ALU.add))
            steps.wait()
            steps.did(dve.tensor_tensor(x_sq[:, 0:XC // 2], x_sq[:, 0:XC // 2], x_sq[:, XC // 2:XC], ALU.add))
            steps.wait()
            dve.tensor_tensor(sq[:, :], x_sq[:, 0:SEQ], x_sq[:, SEQ:2 * SEQ], ALU.add).then_inc(sumsq_ready, 1)
            dve.wait_ge(const_ready, 1)
            dve.tensor_copy(ident_r[:, :], ident[:, :])
            dve.tensor_copy(ntri_r[:, :], ntri[:, :])
            dve.tensor_copy(nones_r[:, :], nones[:, :])
            steps.did(dve.tensor_copy(nmask_r[:, :], nmask[:, :]))
            dve.wait_ge(lb_exp, 1)
            steps.did(dve.tensor_tensor(lb[:, 2 * HEADS:3 * HEADS], lb[:, 0:HEADS], lb[:, HEADS:2 * HEADS], ALU.add))
            steps.wait()
            steps.did(dve.reciprocal(lb[:, 3 * HEADS:4 * HEADS], lb[:, 2 * HEADS:3 * HEADS]))
            steps.wait()
            steps.did(dve.tensor_tensor(lb[:, 0:HEADS], lb[:, 0:HEADS], lb[:, 3 * HEADS:4 * HEADS], ALU.mult))
            steps.wait()
            steps.did(dve.tensor_scalar(lb[:, HEADS:2 * HEADS], lb[:, 0:HEADS], -1.0, 1.0, ALU.mult, ALU.add))
            STEPS0 = steps.n

            def mean_square(psum, width, done):
                dve.tensor_scalar(ms[:, :], psum[:, :], 1.0 / width, EPS, ALU.mult, ALU.add).then_inc(done, 1)

            def newton(st, out):
                st.did(dve.tensor_tensor(tmp[:, :], rs[:, :], rs[:, :], ALU.mult))
                st.wait()
                st.did(dve.tensor_tensor(tmp[:, :], tmp[:, :], ms[:, :], ALU.mult))
                st.wait()
                st.did(dve.tensor_scalar(tmp[:, :], tmp[:, :], -0.5, 1.5, ALU.mult, ALU.add))
                st.wait()
                st.did(dve.tensor_tensor(out, tmp[:, :], rs[:, :], ALU.mult))
                st.wait()

            rms_steps = Steps(dve, rms_step)

            def token_factor(k, psum):
                dve.wait_ge(rms_sum, k)
                mean_square(psum, DM, rms_ms)
                dve.wait_ge(rms_rs, k)
                newton(rms_steps, r_tok[:, :])

            def level(L):
                m = 1 << L
                X = halves(xl[:, L * SEQ:(L + 1) * SEQ], m)
                F_, G_ = halves(pre, m), halves(suf, m)
                Q, K = halves(qn, m), halves(kn, m)
                g = SEQ // (2 * m)
                if L == 0:
                    steps.did(dve.tensor_copy(G_[:, :, 0, :], F_[:, :, 1, :]))
                    steps.did(dve.tensor_copy(X[:, :, 0, :], K[:, :, 0, :]))
                else:
                    steps.did(dve.tensor_tensor(X[:, :, 0, :], K[:, :, 0, :], G_[:, :, 0, :], ALU.mult))
                    steps.did(dve.tensor_tensor(G_[:, :, 0, :], G_[:, :, 0, :],
                                                F_[:, :, 1, m - 1:m].broadcast_to((P, g, m)), ALU.mult))
                steps.did(dve.tensor_tensor(X[:, :, 1, :], Q[:, :, 1, :], F_[:, :, 1, :], ALU.mult))
                steps.wait(1)
                steps.did(dve.tensor_tensor(F_[:, :, 1, :], F_[:, :, 1, :],
                                            F_[:, :, 0, m - 1:m].broadcast_to((P, g, m)), ALU.mult))
                steps.wait()

            def select(rnd):
                for L in ROUND[rnd]:
                    m, g = 1 << L, 64 >> L
                    zb, at_ = LEVEL_AT[L]
                    mask = lmask[:, L * 64:(L + 1) * 64].rearrange("p (j r) -> p j r", j=g) \
                        .bitcast(I32).unsqueeze(1).broadcast_to((P, NB, g, m))
                    data = Z[zb][:, at_:at_ + 256].rearrange("p (b j r) -> p b j r", b=NB, j=g)
                    ins = dve.copy_predicated(diagonal(m), mask, data)
                    if rnd == 0 or L != ROUND[rnd][-1]:
                        steps.did(ins)
                        steps.wait()
                        dve.memset(wait_cell[:, :], 0.0)
                if rnd == 0:
                    mask = ident[:, :].bitcast(I32).unsqueeze(1).broadcast_to((P, NB, P))
                    ins = dve.copy_predicated(diagonal(0), mask,
                                              Z[2][:, :].rearrange("p (b t) -> p b t", b=NB))
                ins.then_inc(sel_ready, 1)

            def phase1_body(i):
                for hh in range(HEADS_PER_BODY):
                    def per(a, b):
                        return i * (HEADS_PER_BODY * a) + (hh * a + b)

                    def take(t, out):
                        dve.wait_ge(unit_done, per(HEAD_UNITS, WSLOTS + 2 * t + 2))
                        dve.tensor_tensor(out, bank[(hh * HEAD_TILES + t) % 2][:, :], r_tok[:, :],
                                          ALU.mult).then_inc(tile_out, 1)

                    def normed(k, x, gain):
                        dve.wait_ge(rs_ready, per(3, k))
                        newton(steps, tmp[:, :])
                        return dve.scalar_tensor_tensor(out=x, in0=x, scalar=gain, in1=tmp[:, :],
                                                        op0=ALU.mult, op1=ALU.mult)

                    def gate_out(t):
                        j = (t - 7) % 2
                        stores = per(32, 16 * ((t - 7) // 2))
                        if not isinstance(stores, int) or stores:
                            dve.wait_ge(gate_stored[j], stores)
                        take(t, g_out[j][:, :])

                    late = int(isinstance(i, int) and hh == 0)
                    for p in range(HEAD_UNITS):
                        split_ahead(0, i, BODY1, hh * HEAD_UNITS + p)
                        if p == 1 + late:
                            if late:
                                token_factor(1, misc_b)
                            take(0, qn[:, :])
                        if p == 3:
                            take(1, kn[:, :])
                        if p == 3 + late:
                            normed(1, qn[:, :], gq_s[:, :]).then_inc(qk_ready, 1)
                        if p in (2 + late, 4, 18):
                            k = {2 + late: 1, 4: 2, 18: 3}[p]
                            dve.wait_ge(ssq_done, per(3, k))
                            mean_square(misc_a, P, ms_ready)
                        if p == 5:
                            take(2, v_in[:, :])
                            normed(2, kn[:, :], col(par, P_GK)).then_inc(qk_ready, 1)
                        if p == 7:
                            take(3, pre[:, :])
                            dve.wait_ge(log1p_ready, per(1, 1))
                            for b in range(NB):
                                ins = dve.scalar_tensor_tensor(out=sp[:, ROW[b]:ROW[b + 1]], in0=Z[b][:, b * P:SEQ],
                                                               scalar=0.0, in1=za[:, ROW[b]:ROW[b + 1]],
                                                               op0=ALU.max, op1=ALU.add)
                            ins.then_inc(sp_ready, 1)
                        if p == 8:
                            dve.wait_ge(sp_hi_ready, per(1, 1))
                            dve.tensor_tensor(sp_lo[:, :], sp[:, :], sp_hi[:, :].bitcast(F32),
                                              ALU.subtract).then_inc(sp_lo_ready, 1)
                        if p == 9:
                            take(4, qn[:, :])
                            dve.memset(suf[:, :], 1.0)
                        if p == 10:
                            dve.wait_ge(sig_ready, per(3, 1))
                            steps.did(dve.tensor_scalar(pre[:, :], pre[:, :], col(lb, per(1, HEADS)),
                                                        col(lb, per(1, 0)), ALU.mult, ALU.add))
                            dve.wait_ge(sig_ready, per(3, 2))
                            dve.tensor_tensor(qn[:, :], qn[:, :], rs[:, :], ALU.mult).then_inc(silu_done, 1)
                            steps.wait()
                            steps.did(dve.tensor_scalar(kn[:, :], pre[:, :], -1.0, 1.0, ALU.mult, ALU.add))
                            steps.wait()
                            dve.wait_ge(silu_done, per(2, 1))
                        if p == 11:
                            take(5, v_in[:, :])
                            level(0)
                            level(1)
                        if p == 12:
                            level(2)
                            level(3)
                            dve.sem_inc(xl_ready, 1)
                        if p == 13:
                            take(6, og[:, :])
                            level(4)
                            level(5)
                        if p == 14:
                            dve.wait_ge(lev_done, per(2, 1))
                            dve.wait_ge(mix_done, per(2, 1))
                            dve.wait_ge(sig_ready, per(3, 3))
                            dve.tensor_tensor(og[:, :], og[:, :], rs[:, :], ALU.mult).then_inc(silu_done, 1)
                            select(0)
                            level(6)
                            steps.did(dve.tensor_tensor(cq[:, 3 * P:4 * P], qn[:, 2 * P:3 * P], pre[:, 2 * P:3 * P], ALU.mult))
                            steps.did(dve.tensor_tensor(cq[:, 5 * P:6 * P], qn[:, 3 * P:4 * P], pre[:, 3 * P:4 * P], ALU.mult))
                            steps.did(dve.tensor_tensor(cq[:, 0:P], qn[:, P:2 * P], pre[:, P:2 * P], ALU.mult))
                            steps.did(dve.tensor_tensor(kc[:, 0:3 * P], kn[:, 0:3 * P], suf[:, 0:3 * P], ALU.mult))
                            steps.wait(2)
                            steps.did(dve.tensor_scalar(cq[:, 4 * P:5 * P], cq[:, 5 * P:6 * P],
                                                        pre[:, 3 * P - 1:3 * P], None, ALU.mult))
                            steps.did(dve.tensor_scalar(cq[:, P:2 * P], cq[:, 3 * P:4 * P],
                                                        pre[:, 2 * P - 1:2 * P], None, ALU.mult))
                            steps.wait()
                            dve.tensor_scalar(cq[:, 2 * P:3 * P], cq[:, 4 * P:5 * P],
                                              pre[:, 2 * P - 1:2 * P], None, ALU.mult).then_inc(xl_ready, 1)
                        if p == 16:
                            dve.wait_ge(lev_done, per(2, 2))
                            gate_out(7)
                            select(1)
                        if p == 17:
                            gate_out(8)
                        if p == 19:
                            yb = cols(y_raw, per(1, HEADS))
                            steps.did(normed(3, yb, col(par, P_GH)))
                            steps.wait()
                            dve.wait_ge(silu_done, per(2, 2))
                            dve.tensor_tensor(yb, yb, og[:, :], ALU.mult).then_inc(yb_ready, 1)
                            gate_out(9)
                        if p == 21:
                            gate_out(10)

            phase1_body(0)
            assert steps.n - STEPS0 == DVE_STEPS1, steps.n - STEPS0
            with dve.Fori(1, HEADS // HEADS_PER_BODY) as i:
                steps.base, steps.n = i * DVE_STEPS1, STEPS0
                phase1_body(i)
                assert steps.n == STEPS0 + DVE_STEPS1
            steps.base, steps.n = 0, STEPS0 + DVE_STEPS1 * (HEADS // HEADS_PER_BODY)

            YC = GROUP * SEQ
            for c in range(4):
                dve.wait_ge(y_hi_ready, c + 1)
                if c == 2:
                    dve.wait_ge(yb_ready, HEADS)
                dve.tensor_tensor(y_lo[:, c * YC:(c + 1) * YC], y_raw[:, c * YC:(c + 1) * YC],
                                  y_hi[:, c * YC:(c + 1) * YC].bitcast(F32), ALU.subtract).then_inc(y_ready, 1)
            step2 = steps.n
            with dve.Fori(0, KT // 2) as i:
                for c in range(2):
                    for p in range(2):
                        split_ahead(START2, i, 2 * 2, 2 * c + p)
                        g = g_in[c][:, p * SEQ:(p + 1) * SEQ]
                        if p == 0:
                            dve.wait_ge(gate_sig, i * 2 + (c + 1))
                        dve.wait_ge(unit_done, i * 4 + (WSLOTS + START2 + 2 * c + p + 1))
                        dve.tensor_tensor((tmp, og)[p][:, :], bank[BANKS2[2 * c + p]][:, :], g,
                                          ALU.mult).then_inc(tile_out, 1)
                        if p == 1:
                            mr = cols(m_raw, i * 2 + c)
                            dve.wait_ge(tile_out, i * 4 + (2 + TILES2 + 2 * c + 2))
                            dve.tensor_tensor(mr, tmp[:, :], og[:, :], ALU.add).then_inc(m_raw_ready, 1)
                            dve.wait_ge(m_hi_ready, i * 2 + (c + 1))
                            dve.wait_ge(m_raw_ready, i * 2 + (c + 1))
                            dve.tensor_tensor(cols(m_lo, i * 2 + c), mr, cols(m_hi, i * 2 + c).bitcast(F32),
                                              ALU.subtract).then_inc(m_ready, 1)

            steps.did(dve.memset(og[:, :], 0.0))
            steps.wait()
            acc0 = steps.n

            def phase3_body(i):
                steps.base, steps.n = i * 2, acc0
                for c in range(2):
                    for p in range(2):
                        split_ahead(START3, i, 2 * 2, 2 * c + p)
                        if p == 1:
                            dve.wait_ge(xr_in[c], i * 16 + 16)
                            if not isinstance(i, int):
                                dve.wait_ge(h_stored[c], i * 16)
                            dve.wait_ge(unit_done, i * 4 + (WSLOTS + START3 + 2 * c + 2))
                            dve.tensor_tensor(hb[c][:, :], bank[BANKS3[c]][:, :], xr[c][:, :],
                                              ALU.add).then_inc(tile_out, 1)
                            dve.wait_ge(v_hi_ready, i * 2 + (c + 1))
                            dve.wait_ge(tile_out, i * 2 + (2 + TILES3 + c + 1))
                            dve.scalar_tensor_tensor(out=cols(v_lo, i * 2 + c), in0=hb[c][:, :],
                                                     scalar=col(par, i * 2 + (P_FFN + c)),
                                                     in1=cols(v_hi, i * 2 + c).bitcast(F32), op0=ALU.mult,
                                                     op1=ALU.subtract).then_inc(v_ready, 1)
                            dve.wait_ge(h_sq_ready, i * 2 + (c + 1))
                            steps.wait()
                            steps.did(dve.tensor_tensor(og[:, :], og[:, :], sq[:, :], ALU.add))

            phase3_body(0)
            with dve.Fori(1, KT // 2) as i:
                phase3_body(i)
            steps.base, steps.n = 0, acc0 + KT
            steps.wait()
            dve.tensor_copy(tmp[:, :], og[:, :]).then_inc(sumsq_ready, 1)

            dve.memset(a_pad[0][:, 0:PAD], 0.0)
            dve.memset(a_pad[1][:, 0:PAD], 0.0).then_inc(pad_ready, 1)
            dve.wait_ge(pad_ready, 1)

            def take_up(unit, t_bank, which):
                dve.wait_ge(unit_done, unit)
                dve.tensor_tensor(a_pad[which][:, PAD:PAD + SEQ], bank[BANKS4[t_bank]][:, :], r_tok[:, :],
                                  ALU.mult).then_inc(tile_out, 1)

            def conv_rest(which, conv_col, started, out_wait):
                y = (y_gate, y_val)[which]
                dve.wait_ge(conv_start, started)
                dve.wait_ge(tile_out, out_wait)
                steps.did(dve.scalar_tensor_tensor(out=y[:, :], in0=a_pad[which][:, PAD - 1:PAD - 1 + SEQ],
                                                   scalar=col(par, conv_col + 1), in1=y[:, :],
                                                   op0=ALU.mult, op1=ALU.add))
                steps.wait()
                return dve.scalar_tensor_tensor(out=y[:, :], in0=a_pad[which][:, 0:SEQ],
                                                scalar=col(par, conv_col), in1=y[:, :],
                                                op0=ALU.mult, op1=ALU.add)

            def up_slot(p, par_g, q0, t0, u0, tb):
                f, r = divmod(p, 4)
                if r == 1 and f < GROUP:
                    if f > 0:
                        k = par_g * GROUP + f - 1
                        dve.wait_ge(s_hi_ready, q0 + f)
                        lo_part(k)
                    take_up(u0 + (WSLOTS + p + 1), (tb + 2 * f) % 8, 0)
                if r == 1 and f == GROUP:
                    k = par_g * GROUP + f - 1
                    dve.wait_ge(s_hi_ready, q0 + f)
                    lo_part(k)
                if r == 2 and f < GROUP:
                    conv_rest(0, (q0 + f) * 4 + P_CONV, q0 * 2 + (2 * f + 1),
                              t0 + (2 + 2 * f + 1)).then_inc(conv_ready, 1)
                if r == 3 and f < GROUP:
                    take_up(u0 + (WSLOTS + p + 1), (tb + 2 * f + 1) % 8, 1)
                if r == 0 and f > 0:
                    k = par_g * GROUP + f - 1
                    steps.did(conv_rest(1, (q0 + f - 1) * 4 + (P_CONV + 4 * FT), q0 * 2 + 2 * f,
                                        t0 + (2 + 2 * f)))
                    steps.wait()
                    dve.wait_ge(silu_ready, q0 + f)
                    dve.tensor_tensor(cols(s_raw, k), y_gate[:, :], y_val[:, :], ALU.mult).then_inc(s_raw_ready, 1)

            def lo_part(k):
                dve.tensor_tensor(cols(s_lo, k), cols(s_raw, k), cols(s_hi, k).bitcast(F32),
                                  ALU.subtract).then_inc(s_ready, 1)

            def take_down(d, unit, tb):
                dve.wait_ge(unit_done, unit)
                for o in range(2):
                    c = 2 * d + o
                    dve.tensor_tensor(cols(h_acc, c), bank[BANKS4[(tb + c) % 8]][:, :], cols(h_acc, c),
                                      ALU.add).then_inc(tile_out, 1)

            steps4 = steps.n
            for p in range(UP_UNITS):
                split_ahead(START4, 0, UP_UNITS, p)
                if p == 1:
                    token_factor(2, bank[1])
                up_slot(p, 0, 0, TILES4, START4, 0)
            up_slot(UP_UNITS, 0, 0, TILES4, START4, 0)
            up_slot(UP_UNITS + 1, 0, 0, TILES4, START4, 0)
            dve.wait_ge(h_back, 16)
            per_group = steps.n - steps4
            with dve.Fori(0, (GROUPS - 1) // 2) as i:
                steps.base, steps.n = i * (2 * per_group), steps4 + per_group
                for gg in range(2):
                    u0 = i * (2 * GROUP_UNITS) + (BODY4 + gg * GROUP_UNITS)
                    t0 = i * (2 * GROUP_TILES) + (TILES_BODY4 + gg * GROUP_TILES)
                    for p in range(GROUP_UNITS):
                        split_ahead(BODY4, i, 2 * GROUP_UNITS, gg * GROUP_UNITS + p)
                        if p <= UP_UNITS + 1:
                            up_slot(p, (1 + gg) % 2, i * (2 * GROUP) + GROUP * (1 + gg), t0, u0, gg * GROUP_TILES)
                        if p >= UP_UNITS:
                            take_down(p - UP_UNITS, u0 + (WSLOTS + p + 1), gg * GROUP_TILES + 2 * GROUP)
            for p in range(DOWN_UNITS):
                split_ahead(LAST_DOWN, 0, DOWN_UNITS, p)
                take_down(p, WSLOTS + LAST_DOWN + p + 1, 0)

        @block.tensor
        def _(pe):
            pe.sem_inc(unit_done, WSLOTS)

            def three(out, slot, kk, hi, lo, first, last):
                wh = w_hi[:, slot * UC + kk * P:slot * UC + (kk + 1) * P]
                wl = w_lo[:, slot * UC + kk * P:slot * UC + (kk + 1) * P]
                nc.tensor.matmul(out, wh, hi, start=first, stop=False)
                nc.tensor.matmul(out, wh, lo, start=False, stop=False)
                return nc.tensor.matmul(out, wl, hi, start=False, stop=last)

            def unit(n, slot, b, hi, lo, k0, first, last, ready=None, step=None):
                pe.wait_ge(w_ready, n + 1)
                for kk in range(UK):
                    if ready is not None and kk % step == 0:
                        pe.wait_ge(ready, (k0 + kk) // step + 1)
                    ins = three(bank[b][:, :], slot, kk, cols(hi, k0 + kk), cols(lo, k0 + kk),
                                first and kk == 0, last and kk == UK - 1)
                ins.then_inc(unit_done, 1)

            def sum_squares(out, x):
                return nc.tensor.matmul(out[:, :], ones[:, :], x, start=True, stop=True)

            def to_tokens():
                for b in range(NB):
                    ins = nc.tensor.transpose(misc_b[:, b * P:(b + 1) * P], v_in[:, b * P:(b + 1) * P], ident[:, :])
                ins.then_inc(vt_done, 1)

            def mix(out):
                for b in range(NB):
                    ins = nc.tensor.matmul(out[:, b * P:SEQ], v_tok[:, b * P:(b + 1) * P],
                                           S[:, b * SEQ + b * P:(b + 1) * SEQ], start=b == 0, stop=b == NB - 1,
                                           skip_group_check=True)
                ins.then_inc(mix_done, 1)

            def levels(rnd):
                for L in ROUND[rnd]:
                    m = 1 << L
                    zb, at_ = LEVEL_AT[L]
                    for b in range(NB):
                        blk = xl[:, L * SEQ + b * P:L * SEQ + (b + 1) * P]
                        right = halves(blk, m, P)[:, :, 1, :]
                        dst = Z[zb][:, at_ + b * 64:at_ + (b + 1) * 64].rearrange("p (j r) -> p j r", r=m)
                        ins = nc.tensor.matmul(dst, blk, right, start=True, stop=True)
                return ins

            def phase1_body(i):
                for hh in range(HEADS_PER_BODY):
                    def per(a, b):
                        return i * (HEADS_PER_BODY * a) + (hh * a + b)

                    late = int(isinstance(i, int) and hh == 0)
                    for p in range(HEAD_UNITS):
                        t, half = divmod(p, 2)
                        if half == 0:
                            pe.wait_ge(tile_out, per(HEAD_TILES, t + 1))
                        unit(per(HEAD_UNITS, p), (hh * HEAD_UNITS + p) % WSLOTS, (hh * HEAD_TILES + t) % 2,
                             u_hi, u_lo, UK * half, half == 0, half == 1,
                             u_ready if isinstance(i, int) and hh == 0 and p < 2 else None, 1)
                        if p == 2 and late:
                            pe.wait_ge(const_step, 1)
                            pe.wait_ge(sumsq_ready, 1)
                            sum_squares(misc_b, sq[:, :]).then_inc(rms_sum, 1)
                        if p in (2 + late, 4, 18):
                            pe.wait_ge(sq_ready, per(3, {2 + late: 1, 4: 2, 18: 3}[p]))
                            sum_squares(misc_a, sq[:, :]).then_inc(ssq_done, 1)
                        if p == 6:
                            if late:
                                pe.wait_ge(const_ready, 1)
                            pe.wait_ge(tile_out, per(HEAD_TILES, 2 + 2 + 1))
                            to_tokens()
                            pe.wait_ge(qk_ready, per(2, 2))
                            for b in range(NB):
                                nc.tensor.matmul(Z[b][:, b * P:SEQ], kn[:, b * P:(b + 1) * P], qn[:, b * P:SEQ],
                                                 start=True, stop=False, skip_group_check=True)
                                ins = nc.tensor.matmul(Z[b][:, b * P:(b + 1) * P], ident_r[:, :], nmask_r[:, :],
                                                       start=False, stop=True, skip_group_check=True)
                            ins.then_inc(z_done, 1)
                        if p == 9:
                            pe.wait_ge(sp_lo_ready, per(1, 1))
                            for b in range(NB):
                                for b2 in range(b, NB):
                                    for part in (sp_hi, sp_lo):
                                        ins = nc.tensor.matmul(Z[b][:, b2 * P:SEQ],
                                                               (ntri_r if b2 == b else nones_r)[:, :],
                                                               part[:, ROW[b2]:ROW[b2 + 1]],
                                                               start=False, stop=True, skip_group_check=True)
                            ins.then_inc(c_done, 1)
                        if p == 10:
                            pe.wait_ge(prob_ready, per(1, 1))
                            pe.wait_ge(vt_ready, per(2, 1))
                            mix(misc_a)
                        if p == 12:
                            pe.wait_ge(tile_out, per(HEAD_TILES, 2 + 5 + 1))
                            to_tokens()
                        if p == 13:
                            pe.wait_ge(xl_ready, per(2, 1))
                            for b in range(NB):
                                nc.tensor.matmul(Z[2][:, b * P:(b + 1) * P], kn[:, b * P:(b + 1) * P],
                                                 qn[:, b * P:(b + 1) * P], start=True, stop=True)
                            levels(0).then_inc(lev_done, 1)
                        if p == 15:
                            pe.wait_ge(xl_ready, per(2, 2))
                            pe.wait_ge(sel_ready, per(2, 1))
                            nc.tensor.matmul(Z[2][:, 0:3 * P], kc[:, 0:P], cq[:, 0:3 * P], start=True, stop=True)
                            nc.tensor.matmul(Z[3][:, 0:2 * P], kc[:, P:2 * P], cq[:, 3 * P:5 * P], start=True, stop=True)
                            nc.tensor.matmul(Z[3][:, 2 * P:3 * P], kc[:, 2 * P:3 * P], cq[:, 5 * P:6 * P],
                                             start=True, stop=True)
                            levels(1).then_inc(lev_done, 1)
                        if p == 17:
                            pe.wait_ge(sel_ready, per(2, 2))
                            pe.wait_ge(cross_ready, per(1, 1))
                            pe.wait_ge(vt_ready, per(2, 2))
                            mix(misc_b)

            phase1_body(0)
            with pe.Fori(1, HEADS // HEADS_PER_BODY) as i:
                phase1_body(i)

            with pe.Fori(0, KT // 2) as i:
                for c in range(2):
                    for br in range(2):
                        p = 2 * c + br
                        pe.wait_ge(tile_out, i * 4 + (TILES2 + p - 1))
                        unit(i * 4 + (START2 + p), p, BANKS2[p], y_hi, y_lo, UK * br, True, True, y_ready, GROUP)

            with pe.Fori(0, KT // 2) as i:
                for c in range(2):
                    pe.wait_ge(tile_out, i * 2 + (TILES3 + c + 1))
                    for half in range(2):
                        pe.wait_ge(m_ready, UK * (half + 1))
                        unit(i * 4 + (START3 + 2 * c + half), 2 * c + half, BANKS3[c], m_hi, m_lo, UK * half,
                             half == 0, half == 1)

            def up(n0, t0, tb, sum_h=False):
                for t in range(2 * GROUP):
                    pe.wait_ge(tile_out, t0 + (t + 3 - 8))
                    for half in range(2):
                        p = 2 * t + half
                        unit(n0 + p, p % WSLOTS, BANKS4[(tb + t) % 8], v_hi, v_lo, UK * half, half == 0, half == 1,
                             v_ready if sum_h and t == 0 else None, 1)
                    if sum_h and t == 0:
                        pe.wait_ge(sumsq_ready, 2)
                        sum_squares(bank[1], tmp[:, :]).then_inc(rms_sum, 1)

            def down(n0, t0, tb, parity, s_wait):
                pe.wait_ge(s_ready, s_wait)
                for d in range(DOWN_UNITS):
                    pe.wait_ge(w_ready, n0 + (d + 1))
                    for o in range(2):
                        t = 2 * d + o
                        pe.wait_ge(tile_out, t0 + (t + 3 - 8))
                        for kk in range(GROUP):
                            k = parity * GROUP + kk
                            ins = three(bank[BANKS4[(tb + t) % 8]][:, :], d % WSLOTS, o * GROUP + kk,
                                        cols(s_hi, k), cols(s_lo, k), kk == 0, kk == GROUP - 1)
                    ins.then_inc(unit_done, 1)

            up(START4, TILES4, 0, True)
            with pe.Fori(0, (GROUPS - 1) // 2) as i:
                for gg in range(2):
                    n0 = i * (2 * GROUP_UNITS) + (BODY4 + gg * GROUP_UNITS)
                    t0 = i * (2 * GROUP_TILES) + (TILES_BODY4 + gg * GROUP_TILES)
                    up(n0, t0, gg * GROUP_TILES)
                    down(n0 + UP_UNITS, t0 + 2 * GROUP, gg * GROUP_TILES + 2 * GROUP, gg,
                         i * (2 * GROUP) + GROUP * (1 + gg))
            down(LAST_DOWN, TILES_LAST, 0, (GROUPS - 1) % 2, GROUPS * GROUP)


def column_tiles(w):
    k, n = w.shape
    return w.reshape(k // UC, UK, P, n // P, P).transpose(3, 0, 2, 1, 4).reshape(n // P, k // UC, P, UC)


def weight_stream(w_in, p_a, p_b, w_o, w_up, w_down):
    s = np.empty((UNITS, P, UC), np.float32)
    wi = column_tiles(w_in)
    H = HEADS
    for h in range(H):
        order = [h, H + h, 2 * H + h, 4 * H + h, 3 * H + h, 5 * H + h, 6 * H + h,
                 7 * H + 2 * h, 7 * H + 2 * h + 1, 7 * H + KT + 2 * h, 7 * H + KT + 2 * h + 1]
        for t, c in enumerate(order):
            s[h * HEAD_UNITS + 2 * t:h * HEAD_UNITS + 2 * t + 2] = wi[c]
    s[START2:START3:2] = column_tiles(p_a)[:, 0]
    s[START2 + 1:START3:2] = column_tiles(p_b)[:, 0]
    s[START3:START4] = column_tiles(w_o).reshape(UNITS3, P, UC)
    up = column_tiles(w_up)
    down = w_down.reshape(GROUPS, GROUP, P, DOWN_UNITS, 2, P).transpose(0, 3, 2, 4, 1, 5) \
        .reshape(GROUPS, DOWN_UNITS, P, UC)
    for g in range(GROUPS):
        at = START4 if g == 0 else BODY4 + (g - 1) * GROUP_UNITS
        for f in range(GROUP):
            s[at + 4 * f:at + 4 * f + 2] = up[g * GROUP + f]
            s[at + 4 * f + 2:at + 4 * f + 4] = up[FT + g * GROUP + f]
        to = BODY4 + g * GROUP_UNITS + UP_UNITS if g < GROUPS - 1 else LAST_DOWN
        s[to:to + DOWN_UNITS] = down[g]
    return s


def channels(a):
    return a.reshape(-1, P).T


def kernel(x, g_mix, w_in, g_q, g_k, lb_logits, g_hg_out, p_a, p_b, w_o, g_ffn, w_up, conv_w, conv_b, w_down):
    import concourse.bacc as bacc
    from concourse.bass_utils import run_bass_kernel_spmd

    f = lambda a: np.asarray(a)
    x, g_mix, w_in, g_q, g_k, lb_logits, g_hg_out, p_a, p_b, w_o, g_ffn, w_up, conv_w, conv_b, w_down = map(
        f, (x, g_mix, w_in, g_q, g_k, lb_logits, g_hg_out, p_a, p_b, w_o, g_ffn, w_up, conv_w, conv_b, w_down))
    taps = np.stack([channels(a) for a in (conv_w[0, 0], conv_w[0, 1], conv_w[0, 2], conv_b[0])], axis=2)
    params = np.concatenate([channels(g_mix[0]), channels(g_ffn[0]), taps.reshape(P, -1),
                             channels(lb_logits[0]), channels(lb_logits[1]),
                             channels(g_q[0]), channels(g_k[0]), channels(g_hg_out[0])], axis=1)
    arrays = {
        "x_t": np.ascontiguousarray(x[0].reshape(SEQ, KT, P).transpose(2, 1, 0).reshape(P, KT * SEQ)),
        "wstream": weight_stream(w_in[0], p_a[0], p_b[0], w_o[0], w_up[0], w_down[0]),
        "params": np.ascontiguousarray(params),
    }
    nc = bacc.Bacc("TRN2", target_bir_lowering=False, num_devices=1)
    args = [nc.dram_tensor(n, a.shape, F32, kind="ExternalInput").ap() for n, a in arrays.items()]
    out = nc.dram_tensor("out_t", (P, KT * SEQ), F32, kind="ExternalOutput").ap()
    build_program(nc, *args, out)
    got = run_bass_kernel_spmd(nc, [arrays], core_ids=[0]).results[0]["out_t"]
    return got.reshape(P, KT, SEQ).transpose(2, 1, 0).reshape(1, SEQ, DM)
```
